# Optimizing a Trainium2 kernel written in Bass

```python
import math
import jax, jax.numpy as jnp
from jax import lax
import numpy as np

D_MODEL = 2048
BATCH = 1
SEQ = 256
DEPTH = 2
DEC_BATCH = 8
DEC_SEQ = 8
PAST_LEN = 2048
PAGE_SIZE = 128

M_HEADS = 8
M_DQK = D_MODEL // (2 * M_HEADS)
M_DV = D_MODEL // M_HEADS
M_CHUNK = 64
GATE_CAP = 15.0
H_DK = 128
H_HEADS = D_MODEL // H_DK
H_DV = D_MODEL // H_HEADS
H_FDIM = H_HEADS * H_DK
H_CHUNK = 32
FF_DIM = -(-8 * D_MODEL // (3 * 256)) * 256
N_MLSTM = (DEPTH + 1) // 2
N_HGRN = DEPTH // 2
M_IN = 2 * M_HEADS * M_DQK + 2 * M_HEADS * M_DV + 2 * M_HEADS
H_IN = 2 * H_FDIM + 2 * H_HEADS * H_DV
EPS = 1e-6

kernel_name = 'hybrid_mlstm_hgrn2_step'

def rms_norm(x, g):
    x32 = x.astype(jnp.float32)
    return x32 * lax.rsqrt(jnp.mean(x32 * x32, axis=-1, keepdims=True) + EPS) * g.astype(jnp.float32)

def to_chunks(a, L):
    B, T = a.shape[:2]
    return a.reshape(B, T // L, L, *a.shape[2:]).swapaxes(0, 1)

def from_chunks(a):
    NC, B, L = a.shape[:3]
    return a.swapaxes(0, 1).reshape(B, NC * L, *a.shape[3:])

def soft_cap(z):
    return GATE_CAP * jnp.tanh(z / GATE_CAP)

def mlstm_mixer(h, C0, n0, m0, w_in, b_gates, head_g, w_out):
    B, T, _ = h.shape
    proj = h @ w_in.astype(jnp.float32)
    s1 = M_HEADS * M_DQK
    s2 = M_HEADS * M_DV
    q, k, v, o, ig, fg = jnp.split(proj, [s1, 2 * s1, 2 * s1 + s2, 2 * s1 + 2 * s2, 2 * s1 + 2 * s2 + M_HEADS], axis=-1)
    q = q.reshape(B, T, M_HEADS, M_DQK)
    k = k.reshape(B, T, M_HEADS, M_DQK) * (M_DQK ** -0.5)
    v = v.reshape(B, T, M_HEADS, M_DV)
    b32 = b_gates.astype(jnp.float32)
    ig = soft_cap(ig + b32[:M_HEADS])
    lf = jax.nn.log_sigmoid(soft_cap(fg + b32[M_HEADS:]))
    L = math.gcd(T, M_CHUNK)
    causal = jnp.tril(jnp.ones((L, L), dtype=bool))

    def body(carry, xs):
        C, n, m = carry
        qc, kc, vc, igc, lfc = xs
        b = jnp.cumsum(lfc, axis=1)
        dlog = b[:, :, None, :] - b[:, None, :, :] + igc[:, None, :, :]
        dlog = jnp.where(causal[None, :, :, None], dlog, -jnp.inf)
        inter = b + m[:, None, :]
        m_t = jnp.maximum(inter, jnp.max(dlog, axis=2))
        w_intra = jnp.exp(dlog - m_t[:, :, None, :])
        w_inter = jnp.exp(inter - m_t)
        s = jnp.einsum('bthc,bjhc->btjh', qc, kc) * w_intra
        num = jnp.einsum('btjh,bjhv->bthv', s, vc) + w_inter[..., None] * jnp.einsum('bthc,bhcv->bthv', qc, C)
        den = jnp.sum(s, axis=2) + w_inter * jnp.einsum('bthc,bhc->bth', qc, n)
        hc = num / jnp.maximum(jnp.abs(den), jnp.exp(-m_t))[..., None]
        b_last = b[:, -1]
        g = b_last[:, None, :] - b + igc
        m_new = jnp.maximum(b_last + m, jnp.max(g, axis=1))
        w = jnp.exp(g - m_new[:, None, :])
        decay = jnp.exp(b_last + m - m_new)
        C_new = decay[..., None, None] * C + jnp.einsum('bjh,bjhc,bjhv->bhcv', w, kc, vc)
        n_new = decay[..., None] * n + jnp.einsum('bjh,bjhc->bhc', w, kc)
        return (C_new, n_new, m_new), hc

    carry0 = (C0.astype(jnp.float32), n0.astype(jnp.float32), m0.astype(jnp.float32))
    (C, n, m), hs = lax.scan(body, carry0, (to_chunks(q, L), to_chunks(k, L), to_chunks(v, L), to_chunks(ig, L), to_chunks(lf, L)))
    hs = rms_norm(from_chunks(hs), head_g.reshape(M_HEADS, M_DV))
    out = (hs.reshape(B, T, M_HEADS * M_DV) * jax.nn.sigmoid(o)) @ w_out.astype(jnp.float32)
    return out, C, n, m

def hgrn2_mixer(h, S0, lb, w_in, gn_g, w_out):
    B, T, _ = h.shape
    proj = h @ w_in.astype(jnp.float32)
    q, fpre, iv, g = jnp.split(proj, [H_FDIM, 2 * H_FDIM, 2 * H_FDIM + H_HEADS * H_DV], axis=-1)
    f = lb + (1.0 - lb) * jax.nn.sigmoid(fpre)
    lf = jnp.log(f).reshape(B, T, H_HEADS, H_DK)
    k = (1.0 - f).reshape(B, T, H_HEADS, H_DK)
    q = q.reshape(B, T, H_HEADS, H_DK) * (H_DK ** -0.5)
    iv = iv.reshape(B, T, H_HEADS, H_DV)
    L = math.gcd(T, H_CHUNK)
    causal = jnp.tril(jnp.ones((L, L), dtype=bool))

    def body(S, xs):
        qc, kc, lfc, ic = xs
        A = jnp.cumsum(lfc, axis=1)
        diff = jnp.where(causal[None, :, :, None, None], A[:, :, None] - A[:, None, :], -jnp.inf)
        wd = jnp.exp(diff)
        s = jnp.einsum('bthc,bjhc,btjhc->btjh', qc, kc, wd)
        oc = jnp.einsum('btjh,bjhv->bthv', s, ic) + jnp.einsum('bthc,bhcv->bthv', qc * jnp.exp(A), S)
        A_last = A[:, -1]
        S_new = jnp.exp(A_last)[..., None] * S + jnp.einsum('bjhc,bjhv->bhcv', kc * jnp.exp(A_last[:, None] - A), ic)
        return S_new, oc

    S, os_ = lax.scan(body, S0.astype(jnp.float32), (to_chunks(q, L), to_chunks(k, L), to_chunks(lf, L), to_chunks(iv, L)))
    o = rms_norm(from_chunks(os_), gn_g.reshape(H_HEADS, H_DV)).reshape(B, T, H_HEADS * H_DV)
    out = (o * jax.nn.silu(g)) @ w_out.astype(jnp.float32)
    return out, S

def swiglu_ffn(h, w_up, w_down):
    a, u = jnp.split(h @ w_up.astype(jnp.float32), 2, axis=-1)
    return (jax.nn.silu(a) * u) @ w_down.astype(jnp.float32)

def trunk(x, mC, mn, mm, hS, norm_mix_g, norm_ffn_g, norm_final_g, mlstm_w_in, mlstm_b_gates,
          mlstm_head_norm_g, mlstm_w_out, hgrn_w_in, hgrn_lower_bounds, hgrn_g_norm_g, hgrn_w_out,
          ffn_w_up, ffn_w_down):
    lb_all = jnp.cumsum(jax.nn.softmax(hgrn_lower_bounds.astype(jnp.float32), axis=0), axis=0)
    lb_all = lb_all - lb_all[0]
    Cs, ns, ms, Ss = [], [], [], []
    for i in range(DEPTH):
        h = rms_norm(x, norm_mix_g[i])
        j = i // 2
        if i % 2 == 0:
            out, C, n, m = mlstm_mixer(h, mC[j], mn[j], mm[j], mlstm_w_in[j], mlstm_b_gates[j],
                                       mlstm_head_norm_g[j], mlstm_w_out[j])
            Cs.append(C); ns.append(n); ms.append(m)
        else:
            out, S = hgrn2_mixer(h, hS[j], lb_all[i], hgrn_w_in[j], hgrn_g_norm_g[j], hgrn_w_out[j])
            Ss.append(S)
        x = x + out.astype(x.dtype)
        x = x + swiglu_ffn(rms_norm(x, norm_ffn_g[i]), ffn_w_up[i], ffn_w_down[i]).astype(x.dtype)
    y = rms_norm(x, norm_final_g).astype(x.dtype)
    return y, jnp.stack(Cs), jnp.stack(ns), jnp.stack(ms), jnp.stack(Ss)

def setup_inputs(seed: int = 0) -> dict:
    key = jax.random.key(seed)
    ks = jax.random.split(key, 24)
    nrm = jax.random.normal
    f32 = jnp.float32
    return {
        'x_prompt': nrm(ks[0], (BATCH, SEQ, D_MODEL), f32),
        'x_sample': nrm(ks[1], (DEC_BATCH, DEC_SEQ, D_MODEL), f32),
        'state_mlstm_C': 0.5 * nrm(ks[2], (N_MLSTM, DEC_BATCH, M_HEADS, M_DQK, M_DV), f32),
        'state_mlstm_n': jnp.abs(nrm(ks[3], (N_MLSTM, DEC_BATCH, M_HEADS, M_DQK), f32)),
        'state_mlstm_m': nrm(ks[4], (N_MLSTM, DEC_BATCH, M_HEADS), f32),
        'state_hgrn_S': 0.5 * nrm(ks[5], (N_HGRN, DEC_BATCH, H_HEADS, H_DK, H_DV), f32),
        'norm_mix_g': 1.0 + 0.02 * nrm(ks[6], (DEPTH, D_MODEL), f32),
        'norm_ffn_g': 1.0 + 0.02 * nrm(ks[7], (DEPTH, D_MODEL), f32),
        'norm_final_g': 1.0 + 0.02 * nrm(ks[8], (D_MODEL,), f32),
        'mlstm_w_in': nrm(ks[9], (N_MLSTM, D_MODEL, M_IN), f32) * D_MODEL ** -0.5,
        'mlstm_b_gates': jnp.concatenate([0.1 * nrm(ks[10], (N_MLSTM, M_HEADS), f32),
                                          3.0 + 3.0 * jax.random.uniform(ks[11], (N_MLSTM, M_HEADS), f32)], axis=-1),
        'mlstm_head_norm_g': 1.0 + 0.02 * nrm(ks[12], (N_MLSTM, M_HEADS * M_DV), f32),
        'mlstm_w_out': nrm(ks[13], (N_MLSTM, M_HEADS * M_DV, D_MODEL), f32) * (M_HEADS * M_DV) ** -0.5,
        'hgrn_w_in': nrm(ks[14], (N_HGRN, D_MODEL, H_IN), f32) * D_MODEL ** -0.5,
        'hgrn_lower_bounds': 0.1 * nrm(ks[15], (DEPTH, H_FDIM), f32),
        'hgrn_g_norm_g': 1.0 + 0.02 * nrm(ks[16], (N_HGRN, H_HEADS * H_DV), f32),
        'hgrn_w_out': nrm(ks[17], (N_HGRN, H_HEADS * H_DV, D_MODEL), f32) * (H_HEADS * H_DV) ** -0.5,
        'ffn_w_up': nrm(ks[18], (DEPTH, D_MODEL, 2 * FF_DIM), f32) * D_MODEL ** -0.5,
        'ffn_w_down': nrm(ks[19], (DEPTH, FF_DIM, D_MODEL), f32) * FF_DIM ** -0.5,
    }

def reference(x_prompt, x_sample, state_mlstm_C, state_mlstm_n, state_mlstm_m, state_hgrn_S,
              norm_mix_g, norm_ffn_g, norm_final_g, mlstm_w_in, mlstm_b_gates, mlstm_head_norm_g,
              mlstm_w_out, hgrn_w_in, hgrn_lower_bounds, hgrn_g_norm_g, hgrn_w_out, ffn_w_up, ffn_w_down):
    B = x_prompt.shape[0]
    zC = jnp.zeros((N_MLSTM, B, M_HEADS, M_DQK, M_DV), jnp.float32)
    zn = jnp.zeros((N_MLSTM, B, M_HEADS, M_DQK), jnp.float32)
    zm = jnp.zeros((N_MLSTM, B, M_HEADS), jnp.float32)
    zS = jnp.zeros((N_HGRN, B, H_HEADS, H_DK, H_DV), jnp.float32)
    y_prompt, C_p, n_p, m_p, S_p = trunk(
        x_prompt, zC, zn, zm, zS, norm_mix_g, norm_ffn_g, norm_final_g, mlstm_w_in, mlstm_b_gates,
        mlstm_head_norm_g, mlstm_w_out, hgrn_w_in, hgrn_lower_bounds, hgrn_g_norm_g, hgrn_w_out,
        ffn_w_up, ffn_w_down)
    y_sample, C_s, n_s, m_s, S_s = trunk(
        x_sample, state_mlstm_C, state_mlstm_n, state_mlstm_m, state_hgrn_S, norm_mix_g, norm_ffn_g,
        norm_final_g, mlstm_w_in, mlstm_b_gates, mlstm_head_norm_g, mlstm_w_out, hgrn_w_in,
        hgrn_lower_bounds, hgrn_g_norm_g, hgrn_w_out, ffn_w_up, ffn_w_down)
    return (y_prompt, y_sample, C_p, n_p, m_p, S_p, C_s, n_s, m_s, S_s)


_drawn_inputs = setup_inputs


def setup_inputs(seed=0):
    import zlib

    import numpy as np

    out = dict(_drawn_inputs(seed))
    spreads = {}
    factors = {'norm_final_g': 8.181,
     'mlstm_head_norm_g': 3.888,
     'hgrn_g_norm_g': 21.439,
     'norm_ffn_g': 2.93}
    for name, (base, spread) in spreads.items():
        noise = np.random.default_rng([zlib.crc32(name.encode()), seed]).standard_normal(out[name].shape)
        drawn = base * np.exp(spread * noise) if base else spread * noise
        out[name] = __import__('jax').numpy.asarray(drawn.astype(out[name].dtype))
    for name, factor in factors.items():
        out[name] = (out[name] * factor).astype(out[name].dtype)
    return out
```

```python
from contextlib import ExitStack

import concourse.bass as bass
from concourse import mybir

P = 128
D = 2048
KT = D // P
TP = 256
NB, TB = 8, 8
TS = NB * TB
T = TP + TS
MH, MDV = 8, 256
HH = 16
FF = 5632
GROUPS = ((0, 16), (16, 16), (32, 12))
EPS = 1e-6
CAP = 15.0
SEG = 64
LEVELS = (32, 16, 8, 4, 2, 1)
QK_SCALE = float(P) ** -0.5
FAR = 1e30

F32 = mybir.dt.float32
F32R = mybir.dt.float32r
I8 = mybir.dt.int8
ALU = mybir.AluOpType
ACT = mybir.ActivationFunctionType
EXP_LN_SET = "natural_log_exp_and_others"


class Phase:

    def __init__(self, name, base, iters, per, k, ring, raw_before, weights, rows, columns, banks=2):
        self.name, self.base, self.iters, self.per, self.k = name, base, iters, per, k
        self.ring, self.raw_before, self.weights, self.rows, self.columns = ring, raw_before, weights, rows, columns
        self.banks = banks
        self.end = base + iters * per

    def landed(self, it, s):
        return self.raw_before[s % self.ring] + it * (self.per // self.ring) + s // self.ring + 1


def plan(w_m_in, w_m_out, w_h_in, w_h_out, w_up, w_down):
    phases, raw = [], [0, 0, 0, 0]

    def add(name, iters, per, k, weights, row0, columns, ring=4, banks=2):
        rows = weights.rearrange("(k p) m -> p k m", p=P)[:, row0:row0 + k, :]
        base = phases[-1].end if phases else 0
        phases.append(Phase(name, base, iters, per, k, ring, list(raw), weights, rows, columns, banks))
        for slot in range(ring):
            raw[slot] += iters * per // ring

    def ffn(layer):
        for g, (first, n) in enumerate(GROUPS):
            add(f"up{layer}{g}", n // 2, 4, KT, w_up[layer], 0,
                [((first + s // 2) * P + (s % 2) * FF, 2 * P) for s in range(4)], banks=4)
            add(f"down{layer}{g}", 4, 4, n, w_down[layer], first, [(s * P, 4 * P) for s in range(4)])

    q, k, v, o = 0, MH * P, 2 * MH * P, 2 * MH * P + MH * MDV
    add("m_in", MH, 6, KT, w_m_in, 0,
        [(k, P), (v, MDV), (v + P, MDV), (q, P), (o, MDV), (o + P, MDV)], ring=3)
    add("m_out", 4, 4, KT, w_m_out, 0, [(s * P, 4 * P) for s in range(4)])
    ffn(0)
    add("h_in", HH, 4, KT, w_h_in, 0, [(D, P), (3 * D, P), (0, P), (2 * D, P)])
    add("h_out", 4, 4, KT, w_h_out, 0, [(s * P, 4 * P) for s in range(4)])
    ffn(1)
    return phases


def need(engine, semaphore, value):
    if not isinstance(value, int) or value > 0:
        engine.wait_ge(semaphore, value)


def trunk(nc, x_prompt, x_sample, C_in, n_in, m_in, S_in, norm_mix_g, norm_ffn_g, norm_final_g,
          mlstm_w_in, mlstm_b_gates, mlstm_head_norm_g, mlstm_w_out, hgrn_w_in, hgrn_lower_bounds,
          hgrn_g_norm_g, hgrn_w_out, ffn_w_up, ffn_w_down,
          y_prompt, y_sample, C_prompt, n_prompt, m_prompt, S_prompt, C_out, n_out, m_out, S_out):
    phases = plan(mlstm_w_in[0], mlstm_w_out[0], hgrn_w_in[0], hgrn_w_out[0],
                  [ffn_w_up[0], ffn_w_up[1]], [ffn_w_down[0], ffn_w_down[1]])
    by_name = {p.name: p for p in phases}

    with ExitStack() as ctx:
        ctx.enter_context(nc.allow_non_contiguous_dma(reason="64 stabilisers and 16 biases, one word each"))

        def sb(name, shape, dt=F32):
            return ctx.enter_context(nc.sbuf_tensor(name, shape, dt))

        def sem(name):
            return ctx.enter_context(nc.semaphore(name))

        x = sb("x", [P, KT, T])
        h_hi = sb("h_hi", [P, KT, T], F32R)
        h_lo = sb("h_lo", [P, KT, T], F32R)
        g_hi = sb("g_hi", [P, KT, T], F32R)
        g_lo = sb("g_lo", [P, KT, T], F32R)
        raw = sb("raw", [P, 4, KT * P])
        w_hi = sb("w_hi", [P, 2, KT * P], F32R)
        w_lo = sb("w_lo", [P, 2, KT * P], F32R)

        ident = sb("ident", [P, P])
        ones = sb("ones", [P, P])
        level_mask = sb("level_mask", [P, len(LEVELS) + 1, T], I8)
        seq_mask = sb("seq_mask", [TS, NB])
        restart = sb("restart", [P, T])
        gains = sb("gains", [P, 7 * KT])
        bounds = sb("bounds", [P, 2, KT])
        rstd = sb("rstd", [P, T])
        rstd_cols = sb("rstd_cols", [P, 3])
        eps_col = sb("eps_col", [P, 1])
        n_cols = sb("n_cols", [P, NB, MH])
        n_new = sb("n_new", [P, (NB + 1) * MH])
        gate_cols = sb("gate_cols", [P, 2, 3, MH])
        spread = sb("spread", [P, NB + TS])
        gate_bias = sb("gate_bias", [40, 2])
        m0 = sb("m0", [MH, NB])
        GAIN_MIX, GAIN_FFN, GAIN_FINAL, GAIN_M, GAIN_H = (0, KT), (2 * KT, 3 * KT), 4 * KT, 5 * KT, 6 * KT

        ARENA = 9200
        arena = sb("arena", [P, ARENA])

        class Carve:

            def __init__(self, at=0):
                self.at = at

            def __call__(self, *shape, parts=P):
                n = 1
                for d in shape:
                    n *= d
                assert self.at + n <= ARENA, (self.at, n)
                v = arena[0:parts, self.at:self.at + n]
                self.at += n
                return v.rearrange("p (a b) -> p a b", a=shape[0]) if len(shape) == 2 else v

        NROWS = 2 * T + NB + TS
        R_DECAY, R_INTER, R_EM = T, T + NB, T + NB + TS
        top = Carve(ARENA - (TP + P + TS) - NROWS)
        rows8 = top(NROWS, parts=MH)
        n_stage = arena[0:(NB + 1) * MH, ARENA - (TP + P + TS) - NROWS:][:, 0:P]
        penal = top(TP + P + TS)

        carve = Carve()
        x_tok = carve(3, D)
        vec_rows = carve(P, parts=7 * KT)
        bound_rows = carve(P, parts=2 * KT)
        n_rows = carve(P, parts=TS)
        wg_raw = carve(KT, 2 * MH)
        sumsq = carve(T)
        square = carve(2, T)
        bound_cols = carve(4, KT)
        assert carve.at <= ARENA - (TP + P + TS) - NROWS
        carve = Carve()
        z_gate, t_gate = carve(T), carve(T)
        row_b, row_a, row_m, row_w, sum_restart, max_restart = (carve(T) for _ in range(6))

        carve = Carve()
        kT, qT = carve(T), carve(T)
        vT, oT = carve(2, T), carve(2, T)
        k_tok = carve(3, P)
        v_tok = carve(3, MDV)
        wk = carve(3, P)
        wk_seq = carve(NB, P)
        att = carve(TP + P + TS)
        C_p = carve(MDV)
        em = carve(T)
        qw, qn = carve(TS), carve(TS)
        den = carve(T)
        hs = carve(2, T)
        m_rs = carve(T)
        n_kept = carve(NB)
        row_of_head = carve(NROWS, parts=MH)
        assert carve.at <= ARENA - (TP + P + TS) - NROWS, carve.at
        C = raw[:, 3, :].rearrange("p (b v) -> p b v", b=NB)

        carve = Carve()
        hf, hg, hg_sig, hq, hk, h_logf, hA = (carve(T) for _ in range(7))
        q_exp, k0, q0, hi_T = (carve(T) for _ in range(4))
        k_exp = h_logf
        pair = carve(2, T)
        scores = carve(T)
        scores_far = carve(P)
        q_far = carve(SEG)
        k_last = carve(P)
        i_tok, hk_tok = carve(3, P), carve(3, P)
        hk_seq = carve(NB, P)
        S = carve(NB, P)
        S_p = carve(P)
        gate, gate_before = carve(T), carve(T)
        h_sq, h_rs = carve(T), carve(T)
        h_y = h_sq

        carve = Carve()
        fa, f_sig, f_full = carve(2, T), carve(2, T), carve(2, T)
        fu = carve(T)
        carve = Carve()
        y_tok = carve(3, D)
        y_T = carve(2, T)
        y_end = carve.at
        assert y_end <= ARENA - (TP + P + TS) - NROWS

        bank = [ctx.enter_context(nc.psum_tensor(f"bank{i}", [P, 512], F32)) for i in range(8)]
        MX = bank[2:8]

        raw_landed = [sem(f"raw_landed{i}") for i in range(4)]
        passed = sem("passed")
        hi_done, lo_done = sem("hi_done"), sem("lo_done")
        gemm_done, evac_done = sem("gemm_done"), sem("evac_done")

        X_PARTS = ((0, 4), (4, 10), (10, KT))
        x_landed = [sem(f"x_landed{i}") for i in range(len(X_PARTS))]
        gains_landed, vectors_landed, wg_landed = sem("gains_landed"), sem("vectors_landed"), sem("wg_landed")
        ones_ready, consts_ready, masks_ready = sem("ones_ready"), sem("consts_ready"), sem("masks_ready")
        x_turned, cols_turned, cols_kept = sem("x_turned"), sem("cols_turned"), sem("cols_kept")
        wg_zero, wg_hi_ready, wg_lo_ready = sem("wg_zero"), sem("wg_hi_ready"), sem("wg_lo_ready")
        lb_diff, lb_exp = sem("lb_diff"), sem("lb_exp")
        gates_done = sem("gates_done")
        gates_scaled, gates_capped, gates_summed, gates_exp = sem("gates_scaled"), sem("gates_capped"), sem("gates_summed"), sem("gates_exp")
        rows_turned, rows_kept, m_stored = sem("rows_turned"), sem("rows_kept"), sem("m_stored")

        x_done, x_hi_done, x_sq_done, x_lo_done = sem("x_done"), sem("x_hi_done"), sem("x_sq_done"), sem("x_lo_done")
        sumsq_ready, sum_done, rstd_ready = sem("sumsq_ready"), sem("sum_done"), sem("rstd_ready")

        m_row, m_turned, m_kept, m_expo, m_weights = sem("m_row"), sem("m_turned"), sem("m_kept"), sem("m_expo"), sem("m_weights")
        m_wk, m_vturned, m_vkept, m_qw = sem("m_wk"), sem("m_vturned"), sem("m_vkept"), sem("m_qw")
        m_scores, m_att, m_num, m_abs, m_hs = sem("m_scores"), sem("m_att"), sem("m_num"), sem("m_abs"), sem("m_hs")
        m_sq, m_sig, m_sum, m_rstd, m_gated = sem("m_sq"), sem("m_sig"), sem("m_sum"), sem("m_rstd"), sem("m_gated")
        m_new0, m_new1, m_new2 = sem("m_new0"), sem("m_new1"), sem("m_new2")
        m_C0, m_C1, m_C2 = sem("m_C0"), sem("m_C1"), sem("m_C2")
        C_landed, C_stored = sem("C_landed"), sem("C_stored")
        n_turned, n_done, n_stored = sem("n_turned"), sem("n_done"), sem("n_stored")

        g_fsig, g_f, g_logf = sem("g_fsig"), sem("g_f"), sem("g_logf")
        g_sums, g_exps, g_factors = sem("g_sums"), sem("g_exps"), sem("g_factors")
        g_diff, g_pairexp = [sem(f"g_diff{i}") for i in range(3)], [sem(f"g_pairexp{i}") for i in range(3)]
        g_pair = [sem(f"g_pair{i}") for i in range(3)]
        g_p, g_c = [sem(f"g_products{i}") for i in range(3)], [sem(f"g_copied{i}") for i in range(3)]
        g_ikept, g_kkept, g_kseq, g_o, g_sq, g_sum, g_rstd = (sem("g_" + n) for n in ("ikept", "kkept", "kseq", "o", "sq", "sum", "rstd"))
        g_S, g_full, g_hi_done, g_gated = sem("g_S"), sem("g_full"), sem("g_hi_done"), sem("g_gated")
        S_landed, S_stored = sem("S_landed"), sem("S_stored")

        f_a, f_sig_done, f_hidden = sem("f_a"), sem("f_sig_done"), sem("f_hidden")
        y_gained, y_turned, y_kept = sem("y_gained"), sem("y_turned"), sem("y_kept")
        y_scaled_dve, y_scaled_act, y_stored = sem("y_scaled_dve"), sem("y_scaled_act"), sem("y_stored")

        def apart(engine):
            engine.sem_inc(passed, 1)

        def load_tile(sp, ph, it, s):
            n = ph.base + it * ph.per + s
            base, step = ph.columns[s]
            column = base + it * step if isinstance(it, int) else sp.snap(base + it * step)
            freed = n - 3 + 1
            need(sp, lo_done, freed if isinstance(it, int) else sp.snap(freed))
            if not isinstance(it, int):
                apart(sp)
            sp.dma_start(raw[:, s % ph.ring, 0:ph.k * P].rearrange("p (k m) -> p k m", k=ph.k),
                         ph.rows[:, :, bass.ds(column, P)]).then_inc(raw_landed[s % ph.ring], 16)

        def split_high(act, ph, it, s):
            n = ph.base + it * ph.per + s
            act.wait_ge(raw_landed[s % ph.ring], ph.landed(it, s) * 16)
            need(act, gemm_done, n - 1)
            act.activation(w_hi[:, s % 2, 0:ph.k * P], raw[:, s % ph.ring, 0:ph.k * P],
                           ACT.Copy).then_inc(hi_done, 1)

        def split_low(dve, ph, it, s):
            n = ph.base + it * ph.per + s
            dve.wait_ge(hi_done, n + 1)
            dve.tensor_tensor(w_lo[:, s % 2, 0:ph.k * P], raw[:, s % ph.ring, 0:ph.k * P],
                              w_hi[:, s % 2, 0:ph.k * P].bitcast(F32), ALU.subtract).then_inc(lo_done, 1)

        def product_steps(pe, ph, s, ks, hi, lo, before_k=None):
            out = bank[s % ph.banks][:, 0:T]
            for k in ks:
                if before_k:
                    before_k(k)
                tile_hi = w_hi[:, s % 2, k * P:(k + 1) * P]
                tile_lo = w_lo[:, s % 2, k * P:(k + 1) * P]
                pe.matmul(out, tile_hi, hi[:, k, :], start=(k == 0), stop=False)
                pe.matmul(out, tile_hi, lo[:, k, :], start=False, stop=False)
                last = pe.matmul(out, tile_lo, hi[:, k, :], start=False, stop=(k == ph.k - 1))
            return last

        def products(pe, ph, it, s, hi, lo, before_k=None):
            n = ph.base + it * ph.per + s
            pe.wait_ge(lo_done, n + 1)
            product_steps(pe, ph, s, range(ph.k), hi, lo, before_k).then_inc(gemm_done, 1)

        NORM_GAIN = (GAIN_MIX[0], GAIN_FFN[0], GAIN_MIX[1], GAIN_FFN[1], None)

        def x_tile_act(act, r, j, parity):
            act.wait_ge(x_done, r * KT + j + 1)
            apart(act)
            if NORM_GAIN[r] is not None:
                act.activation(h_hi[:, bass.ds(j, 1), :], x[:, bass.ds(j, 1), :], ACT.Copy,
                               scale=gains[:, bass.ds(NORM_GAIN[r] + j, 1)]).then_inc(x_hi_done, 1)
            need(act, sumsq_ready, r * KT + j - 1)
            apart(act)
            act.activation(square[:, parity, :], x[:, bass.ds(j, 1), :], ACT.Square).then_inc(x_sq_done, 1)

        def x_tile_dve(dve, r, j, parity, first):
            if NORM_GAIN[r] is not None:
                dve.wait_ge(x_hi_done, r * KT + j + 1)
                dve.scalar_tensor_tensor(h_lo[:, bass.ds(j, 1), :], x[:, bass.ds(j, 1), :],
                                         gains[:, bass.ds(NORM_GAIN[r] + j, 1)],
                                         h_hi[:, bass.ds(j, 1), :].bitcast(F32),
                                         ALU.mult, ALU.subtract).then_inc(x_lo_done, 1)
            dve.wait_ge(x_sq_done, r * KT + j + 1)
            if first:
                dve.tensor_scalar(sumsq, square[:, parity, :], 1.0, None, ALU.mult).then_inc(sumsq_ready, 1)
            else:
                dve.tensor_tensor(sumsq, sumsq, square[:, parity, :], ALU.add).then_inc(sumsq_ready, 1)
            dve.drain()
            if r == 4:
                need(dve, y_turned, j - 1)
                apart(dve)
                dve.tensor_scalar(y_T[:, parity:parity + 1, :], x[:, bass.ds(j, 1), :],
                                  gains[:, bass.ds(GAIN_FINAL + j, 1)], None, ALU.mult).then_inc(y_gained, 1)

        def norm_pe(pe, r):
            pe.wait_ge(sumsq_ready, (r + 1) * KT)
            pe.matmul(MX[5][:, 0:T], ones[:, :], sumsq, start=True, stop=True).then_inc(sum_done, 1)

        def norm_act(act, r, evacuated):
            act.preload_act_table_set(EXP_LN_SET)
            need(act, evac_done, evacuated)
            act.wait_ge(sum_done, r + 1)
            act.activation(rstd[:, :], MX[5][:, 0:T], ACT.Ln, scale=1.0 / D, bias=eps_col[:, :])
            act.drain()
            act.activation(rstd[:, :], rstd[:, :], ACT.Exp, scale=-0.5).then_inc(rstd_ready, 1)

        M_IN, M_OUT, H_IN, H_OUT = by_name["m_in"], by_name["m_out"], by_name["h_in"], by_name["h_out"]

        def halves(v, l):
            v = v.rearrange("p (n h r) -> p n h r", h=2, r=l)
            return v[:, :, 0, :], v[:, :, 1, :]

        def level_width(l):
            return T if 2 * l <= TB else TP

        block = ctx.enter_context(nc.Block())

        @block.sync
        def _(sp):
            for q, (j0, j1) in enumerate(X_PARTS):
                for b, (src, n) in enumerate(((x_prompt[0, 0:P, :], P), (x_prompt[0, P:TP, :], P),
                                              (x_sample.rearrange("a b d -> (a b) d"), TS))):
                    part = slice(j0 * P, j1 * P)
                    sp.dma_start(x_tok[0:n, b, part], src[:, part]).then_inc(x_landed[q], 16)
            sp.dma_start(wg_raw, mlstm_w_in[0].rearrange("(k p) m -> p k m", p=P)[:, :, 3 * D:3 * D + 2 * MH]).then_inc(wg_landed, 16)
            for ph in phases:
                for s in range(ph.per):
                    if ph is M_OUT and s == 3:
                        sp.wait_ge(C_stored, MH * 32)
                    load_tile(sp, ph, 0, s)
                if ph.iters > 1:
                    with sp.Fori(1, ph.iters) as it:
                        for s in range(ph.per):
                            load_tile(sp, ph, it, s)
            for part in range(2):
                c = slice(part * D // 2, (part + 1) * D // 2)
                for b, (dst, n) in enumerate(((y_prompt[0, 0:P, :], P), (y_prompt[0, P:TP, :], P),
                                              (y_sample.rearrange("a b d -> (a b) d"), TS))):
                    if b == 1:
                        sp.wait_ge(y_scaled_act, part + 1)
                    else:
                        sp.wait_ge(y_scaled_dve, 2 * part + (1 if b == 0 else 2))
                    sp.dma_start(dst[:, c], y_tok[0:n, b, c]).then_inc(y_stored, 16)
            sp.wait_ge(y_stored, 96)

        @block.gpsimd
        def _(pool):
            C_src, C_dst = C_in[0].rearrange("b h c v -> h c b v"), C_out[0].rearrange("b h c v -> h c b v")
            S_src, S_dst = S_in[0].rearrange("b h c v -> h c b v"), S_out[0].rearrange("b h c v -> h c b v")
            pool.memset(ones[:, :], 1.0)
            pool.drain()
            pool.affine_select(out=ident[:, :], in_=ones[:, :], pattern=[[-1, P]], compare_op=ALU.is_equal,
                               fill=0.0, base=0, channel_multiplier=1).then_inc(ones_ready, 1)
            pool.memset(eps_col[:, :], EPS)
            pool.memset(seq_mask[:, :], 1.0)
            pool.memset(penal, 0.0)
            pool.memset(level_mask[:, :, :], 0)
            pool.drain()
            pool.dma_start(bound_rows, hgrn_lower_bounds.rearrange("l (k p) -> (l k) p", p=P)).then_inc(vectors_landed, 16)
            pool.dma_start(n_rows, n_in[0].rearrange("b h c -> (b h) c")).then_inc(vectors_landed, 16)
            bias = mlstm_b_gates.rearrange("a (g h) -> g h a", g=2)
            pool.dma_start(gate_bias[0:MH, 0:1], bias[0]).then_inc(vectors_landed, 16)
            pool.dma_start(gate_bias[32:32 + MH, 0:1], bias[1]).then_inc(vectors_landed, 16)
            pool.dma_start(m0[:, :], m_in[0].rearrange("b h -> h b")).then_inc(vectors_landed, 16)
            pool.affine_select(out=penal[:, 0:TP], in_=penal[:, 0:TP], pattern=[[1, TP]], compare_op=ALU.is_ge,
                               fill=FAR, base=0, channel_multiplier=-1)
            pool.affine_select(out=penal[:, TP:TP + P], in_=penal[:, TP:TP + P], pattern=[[1, P]],
                               compare_op=ALU.is_ge, fill=FAR, base=0, channel_multiplier=-1)
            tail = penal[0:TS, TP + P:].rearrange("p (b t) -> p b t", b=NB)
            pool.affine_select(out=tail, in_=tail, pattern=[[TB, NB], [1, TB]], compare_op=ALU.is_ge,
                               fill=FAR, base=0, channel_multiplier=-1)
            pool.affine_select(out=seq_mask[:, :], in_=seq_mask[:, :], pattern=[[-TB, NB]], compare_op=ALU.is_ge,
                               fill=0.0, base=0, channel_multiplier=1)
            pool.drain()
            pool.affine_select(out=seq_mask[:, :], in_=seq_mask[:, :], pattern=[[TB, NB]], compare_op=ALU.is_ge,
                               fill=0.0, base=TB - 1, channel_multiplier=-1)
            pool.affine_select(out=tail, in_=tail, pattern=[[-TB, NB], [0, TB]], compare_op=ALU.is_ge,
                               fill=FAR, base=0, channel_multiplier=1)
            pool.memset(restart[:, :], 1.0)
            pool.drain()
            pool.memset(restart[:, 0:TP:SEG], 0.0)
            pool.memset(restart[:, TP:T:TB], 0.0).then_inc(consts_ready, 1)
            pool.dma_start(C, C_src[0]).then_inc(C_landed, 16)
            def level_views(i, l):
                views = []
                for c0, c1, blocks in ((0, TP, TP // P), (TP, T, 1)):
                    if c0 == 0 or 2 * l <= TB:
                        v = level_mask[:, i, c0:c1].rearrange("p (n h r) -> p n h r", h=2, r=l)[:, :, 1, :]
                        n = min(P, c1 - c0) // (2 * l)
                        if blocks > 1:
                            v = level_mask[:, i, c0:c1].rearrange("p (a n h r) -> p a n h r", a=blocks, h=2, r=l)[:, :, :, 1, :]
                        views.append((v, blocks, n))
                return views
            levels = [(v, blocks, n, l) for i, l in enumerate(LEVELS) for v, blocks, n in level_views(i, l)]
            for v, blocks, n, l in levels:
                pool.memset(v, 1)
            diag = level_mask[:, len(LEVELS), :]
            pool.memset(diag, 1)
            pool.drain()
            for v, blocks, n, l in levels:
                outer = [[0, blocks]] if blocks > 1 else []
                pool.affine_select(out=v, in_=v, pattern=outer + [[-2 * l, n], [0, l]], compare_op=ALU.is_ge,
                                   fill=0.0, base=0, channel_multiplier=1)
            pool.affine_select(out=diag[:, 0:TP], in_=diag[:, 0:TP], pattern=[[0, 2], [-1, P]],
                               compare_op=ALU.is_equal, fill=0.0, base=0, channel_multiplier=1)
            pool.affine_select(out=diag[:, TP:T], in_=diag[:, TP:T], pattern=[[-1, TS]],
                               compare_op=ALU.is_equal, fill=0.0, base=0, channel_multiplier=1)
            pool.drain()
            for v, blocks, n, l in levels:
                outer = [[0, blocks]] if blocks > 1 else []
                last = pool.affine_select(out=v, in_=v, pattern=outer + [[2 * l, n], [0, l]], compare_op=ALU.is_ge,
                                          fill=0.0, base=l - 1, channel_multiplier=-1)
            last.then_inc(masks_ready, 1)

            pool.wait_ge(gates_summed, 1)
            pool.dma_start(m_prompt[0].rearrange("a h -> h a"), row_m[0:MH, TP - 1:TP]).then_inc(m_stored, 16)
            pool.dma_start(m_out[0].rearrange("b h -> h b"), row_m[0:MH, TP + TB - 1:T:TB]).then_inc(m_stored, 16)
            pool.wait_ge(m_stored, 32)

            def store_C(h):
                pool.wait_ge(m_C2, h + 1)
                apart(pool)
                at = h
                pool.dma_start(C_dst[bass.ds(at, 1)], C).then_inc(C_stored, 16)
                pool.dma_start(C_prompt[0, 0, bass.ds(at, 1)], C_p).then_inc(C_stored, 16)
                pool.wait_ge(C_stored, 32 * (h + 1))
                apart(pool)

            with pool.Fori(0, MH - 1) as h:
                store_C(h)
                pool.dma_start(C, C_src[bass.ds(h + 1, 1)]).then_inc(C_landed, 16)
            store_C(MH - 1)
            pool.wait_ge(n_done, 1)
            pool.dma_start(n_out[0].rearrange("b h c -> (b h) c"), n_stage[0:TS, :]).then_inc(n_stored, 16)
            pool.dma_start(n_prompt[0, 0], n_stage[TS:TS + MH, :]).then_inc(n_stored, 16)
            pool.wait_ge(n_stored, 32)

            pool.wait_ge(evac_done, H_IN.base + 1)
            pool.dma_start(S, S_src[0]).then_inc(S_landed, 16)

            def store_S(h):
                pool.wait_ge(g_S, h + 1)
                apart(pool)
                at = h
                pool.dma_start(S_dst[bass.ds(at, 1)], S).then_inc(S_stored, 16)
                pool.dma_start(S_prompt[0, 0, bass.ds(at, 1)], S_p).then_inc(S_stored, 16)
                pool.wait_ge(S_stored, 32 * (h + 1))
                apart(pool)

            with pool.Fori(0, HH - 1) as h:
                store_S(h)
                pool.dma_start(S, S_src[bass.ds(h + 1, 1)]).then_inc(S_landed, 16)
            store_S(HH - 1)

        @block.scalar
        def _(act):
            for row, v in ((0, norm_mix_g.rearrange("l (k p) -> (l k) p", p=P)),
                           (2 * KT, norm_ffn_g.rearrange("l (k p) -> (l k) p", p=P)),
                           (4 * KT, norm_final_g.rearrange("(k p) -> k p", p=P)),
                           (5 * KT, mlstm_head_norm_g.rearrange("l (k p) -> (l k) p", p=P)),
                           (6 * KT, hgrn_g_norm_g.rearrange("l (k p) -> (l k) p", p=P))):
                act.dma_start(vec_rows[row:row + v.shape[0], :], v).then_inc(gains_landed, 16)
            act.wait_ge(cols_kept, 1)
            for j in range(KT):
                x_tile_act(act, 0, j, j % 2)
                if j == 0:
                    act.wait_ge(wg_landed, 16)
                    act.wait_ge(wg_zero, 2)
                    wide = w_hi[:, 1, :].rearrange("p (k m) -> p k m", k=KT)
                    act.activation(wide[:, :, 0:MH], wg_raw[:, :, 0:MH], ACT.Copy)
                    act.activation(wide[:, :, 32:32 + MH], wg_raw[:, :, MH:], ACT.Copy).then_inc(wg_hi_ready, 1)
            act.wait_ge(consts_ready, 1)

            def gate_rows():
                act.wait_ge(gates_scaled, 1)
                for p0 in (0, 32):
                    act.activation(t_gate[p0:p0 + MH], z_gate[p0:p0 + MH], ACT.Tanh, scale=1.0 / CAP,
                                   bias=gate_bias[p0:p0 + MH, 1:2])
                act.drain()
                act.preload_act_table_set(EXP_LN_SET)
                act.activation(t_gate[32:32 + MH], t_gate[32:32 + MH], ACT.Exp, scale=-CAP)
                act.drain()
                act.activation(t_gate[32:32 + MH], t_gate[32:32 + MH], ACT.Ln, bias=ones[32:32 + MH, 0:1]).then_inc(gates_capped, 1)
                act.wait_ge(lb_diff, 1)
                act.activation(bound_cols[:, 0:2, :], bound_cols[:, 0:2, :], ACT.Exp).then_inc(lb_exp, 1)
                split_high(act, M_IN, 0, 2)
                act.wait_ge(gates_summed, 1)
                act.activation(rows8[:, R_EM:R_EM + T], row_m[0:MH], ACT.Exp, scale=-1.0)
                act.activation(row_w[0:MH], row_w[0:MH], ACT.Exp)
                act.activation(rows8[:, R_DECAY:R_EM], rows8[:, R_DECAY:R_EM], ACT.Exp).then_inc(gates_exp, 1)

            def m2(h):
                act.wait_ge(m_turned, h + 1)
                need(act, m_C2, h)
                act.activation(k_tok[:, 0:2, :], MX[2][:, 0:2 * P].rearrange("p (a b) -> p a b", a=2), ACT.Copy)
                act.activation(k_tok[0:TS, 2, :], MX[2][0:TS, 2 * P:3 * P], ACT.Copy)
                act.activation(em, MX[1][:, 0:T], ACT.Copy)
                act.preload_act_table_set(EXP_LN_SET)
                act.wait_ge(m_expo, h + 1)
                act.activation(spread[:, :], MX[0][:, T:T + NB + TS], ACT.Copy).then_inc(m_kept, 1)
                act.activation(att[:, 0:TP + P], att[:, 0:TP + P], ACT.Exp, scale=-1.0)
                act.activation(att[0:TS, TP + P:], att[0:TS, TP + P:], ACT.Exp, scale=-1.0).then_inc(m_weights, 1)

            def m4(h):
                act.wait_ge(m_vturned, h + 1)
                for i in range(2):
                    act.activation(v_tok[:, 0:2, i * P:(i + 1) * P],
                                   MX[2 + i][:, 0:2 * P].rearrange("p (a b) -> p a b", a=2), ACT.Copy)
                    last = act.activation(v_tok[0:TS, 2, i * P:(i + 1) * P], MX[2 + i][0:TS, 2 * P:3 * P], ACT.Copy)
                last.then_inc(m_vkept, 1)

            def m6(h):
                act.wait_ge(m_num, h + 1)
                act.activation(den, MX[1][:, 0:T], ACT.Abs).then_inc(m_abs, 1)
                act.wait_ge(evac_done, M_IN.base + 6 * h + 6)
                act.activation(oT, oT, ACT.Sigmoid).then_inc(m_sig, 1)
                act.wait_ge(m_hs, h + 1)
                act.activation(vT, hs, ACT.Square).then_inc(m_sq, 1)

            def m7(h):
                act.preload_act_table_set(EXP_LN_SET)
                act.wait_ge(m_sum, h + 1)
                act.activation(m_rs, MX[1][:, 0:T], ACT.Ln, scale=1.0 / MDV, bias=eps_col[:, :])
                act.drain()
                act.activation(m_rs, m_rs, ACT.Exp, scale=-0.5).then_inc(m_rstd, 1)

            def m_body(it, before):
                for s in range(6):
                    if not (s in (1, 2) and isinstance(it, int)):
                        split_high(act, M_IN, it, s)
                    if s == 0 and isinstance(it, int):
                        act.wait_ge(gates_done, 1)
                        split_high(act, M_IN, it, 1)
                        norm_act(act, 0, 0)
                        gate_rows()
                    if s == 0 and before is not None:
                        m6(before)
                    if s == 1 and before is not None:
                        m7(before)
                    if s == 2:
                        m2(it)
                    if s == 4:
                        m4(it)

            m_body(0, None)
            with act.Fori(1, MH) as it:
                m_body(it, it - 1)

            def keep_y(j, parity):
                act.wait_ge(y_turned, j + 1)
                apart(act)
                tile = MX[parity]
                at = j * P if isinstance(j, int) else act.snap(j * P)
                act.activation(y_tok[:, 0:2, bass.ds(at, P)], tile[:, 0:TP].rearrange("p (b c) -> p b c", b=2), ACT.Copy)
                act.activation(y_tok[0:TS, 2:3, bass.ds(at, P)],
                               tile[0:TS, TP:TP + P].rearrange("p (b c) -> p b c", b=1), ACT.Copy).then_inc(y_kept, 1)

            def x_phase(ph, r, boundary):
                for s in range(4):
                    if not (ph is H_OUT and s == 1):
                        split_high(act, ph, 0, s)
                    if ph is H_OUT and s == 0:
                        split_high(act, ph, 0, 1)
                    if s in boundary:
                        boundary[s]()
                    if s == 1 and ph is H_OUT:
                        act.wait_ge(S_stored, HH * 32)
                    if s and r is not None:
                        x_tile_act(act, r, s - 1, (s - 1) % 2)
                    if s > 1 and r == 4:
                        keep_y(s - 2, s % 2)
                with act.Fori(1, ph.iters) as it:
                    for s in range(4):
                        split_high(act, ph, it, s)
                        if r is not None:
                            x_tile_act(act, r, it * 4 + s - 1, (s - 1) % 2)
                        if r == 4:
                            keep_y(it * 4 + s - 2, s % 2)

            def ffn(layer, r_in, r_out):
                pairs = 0
                for g, (first, n) in enumerate(GROUPS):
                    up, down = by_name[f"up{layer}{g}"], by_name[f"down{layer}{g}"]
                    pairs = layer * (FF // P) + first

                    def gate_sigmoid(it, s):
                        pair = pairs + it * 2 + (s - 1) // 2
                        act.wait_ge(f_a, pair + 1)
                        act.activation(f_sig[:, (s - 1) // 2, :], fa[:, (s - 1) // 2, :], ACT.Sigmoid).then_inc(f_sig_done, 1)

                    for s in range(4):
                        split_high(act, up, 0, s)
                        if g == 0 and s == 0:
                            x_tile_act(act, r_in, KT - 1, (KT - 1) % 2)
                        if g == 0 and s == 1:
                            norm_act(act, r_in, up.base)
                        if s % 2:
                            gate_sigmoid(0, s)
                    with act.Fori(1, up.iters) as it:
                        for s in range(4):
                            split_high(act, up, it, s)
                            if s % 2:
                                gate_sigmoid(it, s)
                    x_phase(down, r_out if g == len(GROUPS) - 1 else None, {})

            x_phase(M_OUT, 1, {0: lambda: m6(MH - 1), 1: lambda: m7(MH - 1)})
            ffn(0, 1, 2)

            def pair_exps(h, i):
                act.wait_ge(g_diff[i], h + 1)
                for u in range(2):
                    l = LEVELS[2 * i + u]
                    first, second = halves(pair[:, u, 0:level_width(l)], l)
                    act.activation(first, first, ACT.Exp, scale=-1.0)
                    last = act.activation(second, second, ACT.Exp)
                last.then_inc(g_pairexp[i], 1)

            def h2(h):
                act.wait_ge(evac_done, H_IN.base + 4 * h + 2)
                act.activation(hf, hf, ACT.Sigmoid)
                act.activation(hg_sig, hg, ACT.Sigmoid).then_inc(g_fsig, 1)

            def h3(h):
                act.preload_act_table_set(EXP_LN_SET)
                act.wait_ge(g_f, h + 1)
                act.activation(h_logf, hf, ACT.Ln).then_inc(g_logf, 1)

            def h4(h):
                need(act, g_S, h)
                act.wait_ge(g_sums, h + 1)
                act.activation(k_exp, k_exp, ACT.Exp)
                act.activation(q_exp, hA, ACT.Exp).then_inc(g_exps, 1)
                pair_exps(h, 0)

            def h5(h):
                act.wait_ge(g_p[0], h + 1)
                act.activation(i_tok[:, 0:2, :], MX[0][:, 0:2 * P].rearrange("p (a b) -> p a b", a=2), ACT.Copy)
                act.activation(i_tok[0:TS, 2, :], MX[0][0:TS, 2 * P:3 * P], ACT.Copy).then_inc(g_ikept, 1)
                pair_exps(h, 1)

            def h6(h):
                act.wait_ge(g_p[1], h + 1)
                act.activation(hk_tok[:, 0:2, :], MX[4][:, 0:2 * P].rearrange("p (a b) -> p a b", a=2), ACT.Copy)
                act.activation(hk_tok[0:TS, 2, :], MX[4][0:TS, 2 * P:3 * P], ACT.Copy).then_inc(g_kkept, 1)
                pair_exps(h, 2)

            def h8(h):
                act.wait_ge(g_o, h + 1)
                act.activation(h_sq, MX[5][:, 0:T], ACT.Square).then_inc(g_sq, 1)

            def h9(h):
                act.preload_act_table_set(EXP_LN_SET)
                act.wait_ge(g_sum, h + 1)
                act.activation(h_rs, MX[4][:, 0:T], ACT.Ln, scale=1.0 / P, bias=eps_col[:, :])
                act.drain()
                act.activation(h_rs, h_rs, ACT.Exp, scale=-0.5).then_inc(g_rstd, 1)
                act.wait_ge(g_full, h + 1)
                apart(act)
                act.activation(g_hi[:, bass.ds(h, 1), :], h_y, ACT.Copy).then_inc(g_hi_done, 1)

            def h_tail(slot, one_back, two_back):
                if slot == 0:
                    if two_back is not None:
                        h8(two_back)
                    if one_back is not None:
                        h4(one_back)
                if slot == 1:
                    if two_back is not None:
                        h9(two_back)
                    if one_back is not None:
                        h5(one_back)
                if slot == 2 and one_back is not None:
                    h6(one_back)

            def h_body(it, one_back, two_back):
                for s in range(4):
                    split_high(act, H_IN, it, s)
                    if s == 0 and one_back is None:
                        x_tile_act(act, 2, KT - 1, (KT - 1) % 2)
                    if s == 1 and one_back is None:
                        norm_act(act, 2, H_IN.base)
                    h_tail(s, one_back, two_back)
                    if s == 2:
                        h2(it)
                    if s == 3:
                        h3(it)

            h_body(0, None, None)
            h_body(1, 0, None)
            with act.Fori(2, HH) as it:
                h_body(it, it - 1, it - 2)

            def h_end():
                for one_back, two_back in ((HH - 1, HH - 2), (None, HH - 1)):
                    for slot in range(4):
                        h_tail(slot, one_back, two_back)

            x_phase(H_OUT, 3, {0: h_end})
            ffn(1, 3, 4)
            x_tile_act(act, 4, KT - 1, (KT - 1) % 2)
            keep_y(KT - 2, (KT - 2) % 2)
            keep_y(KT - 1, (KT - 1) % 2)
            act.preload_act_table_set(EXP_LN_SET)
            act.wait_ge(sum_done, 5)
            for p0, cols in ((P, slice(0, 2)), (TS, slice(2, 3))):
                act.activation(rstd_cols[0:p0, cols], MX[4][0:p0, cols], ACT.Ln, scale=1.0 / D, bias=eps_col[0:p0, :])
            act.drain()
            for p0, cols in ((P, slice(0, 2)), (TS, slice(2, 3))):
                last = act.activation(rstd_cols[0:p0, cols], rstd_cols[0:p0, cols], ACT.Exp, scale=-0.5)
            last.then_inc(rstd_ready, 1)
            act.drain()
            for part in range(2):
                c = slice(part * D // 2, (part + 1) * D // 2)
                act.activation(y_tok[:, 1, c], y_tok[:, 1, c], ACT.Copy, scale=rstd_cols[:, 1:2]).then_inc(y_scaled_act, 1)

        @block.vector
        def _(dve):
            dve.memset(w_hi[:, 1, :].bitcast(F32), 0.0).then_inc(wg_zero, 1)
            dve.memset(w_lo[:, 1, :].bitcast(F32), 0.0).then_inc(wg_zero, 1)
            dve.wait_ge(cols_turned, 1)
            dve.tensor_copy(gains[:, :], bank[2][:, 0:7 * KT]).then_inc(cols_kept, 1)
            dve.drain()

            for j in range(KT + 1):
                if j < KT:
                    dve.wait_ge(x_turned, j + 1)
                    dve.tensor_copy(x[:, j, :], bank[j % 2][:, 0:T]).then_inc(x_done, 1)
                if j > 0:
                    x_tile_dve(dve, 0, j - 1, (j - 1) % 2, j == 1)
                if j == 1:
                    dve.wait_ge(wg_hi_ready, 1)
                    lo_wide = w_lo[:, 1, :].rearrange("p (k m) -> p k m", k=KT)
                    hi_wide = w_hi[:, 1, :].rearrange("p (k m) -> p k m", k=KT).bitcast(F32)
                    dve.tensor_tensor(lo_wide[:, :, 0:MH], wg_raw[:, :, 0:MH], hi_wide[:, :, 0:MH], ALU.subtract)
                    dve.tensor_tensor(lo_wide[:, :, 32:32 + MH], wg_raw[:, :, MH:], hi_wide[:, :, 32:32 + MH],
                                      ALU.subtract).then_inc(wg_lo_ready, 1)
            def gate_rows():
                dve.memset(sum_restart[0:MH], 1.0)
                dve.memset(max_restart[0:MH], 0.0)
                dve.drain()
                for v, fill in ((sum_restart, 0.0), (max_restart, -FAR)):
                    dve.memset(v[0:MH, 0:1], fill)
                    dve.memset(v[0:MH, TP:T:TB], fill)
                dve.wait_ge(cols_turned, 2)
                dve.tensor_copy(bound_cols[:, 2:4, :], bank[3][:, 0:2 * KT].rearrange("p (l k) -> p l k", l=2))
                dve.tensor_copy(n_cols[:, :, :], bank[3][:, 2 * KT:2 * KT + TS].rearrange("p (b h) -> p b h", b=NB))
                dve.wait_ge(vectors_landed, 80)
                for p0 in (0, 32):
                    dve.tensor_scalar(gate_bias[p0:p0 + MH, 1:2], gate_bias[p0:p0 + MH, 0:1], 1.0 / CAP, None, ALU.mult)
                dve.wait_ge(rstd_ready, 1)
                for p0 in (0, 32):
                    last = dve.tensor_tensor(z_gate[p0:p0 + MH], MX[0][p0:p0 + MH, 0:T], rstd[p0:p0 + MH, :], ALU.mult)
                last.then_inc(gates_scaled, 1)
                dve.drain()
                dve.tensor_tensor(bounds[:, 0, :], bound_cols[:, 2, :], bound_cols[:, 3, :], ALU.max)
                dve.drain()
                for l in range(2):
                    last = dve.tensor_tensor(bound_cols[:, l, :], bound_cols[:, 2 + l, :], bounds[:, 0, :], ALU.subtract)
                last.then_inc(lb_diff, 1)
                dve.wait_ge(gates_capped, 1)
                dve.tensor_scalar(row_w[0:MH], t_gate[32:32 + MH], -1.0, None, ALU.mult)
                dve.tensor_scalar(row_a[0:MH], t_gate[0:MH], CAP, None, ALU.mult)
                dve.drain()
                dve.tensor_tensor_scan(row_b[0:MH], sum_restart[0:MH], row_w[0:MH], 0.0, ALU.mult, ALU.add)
                dve.drain()
                dve.tensor_tensor(row_a[0:MH], row_a[0:MH], row_b[0:MH], ALU.subtract)
                dve.drain()
                dve.tensor_copy(row_m[0:MH], row_a[0:MH])
                dve.drain()
                dve.tensor_scalar(row_m[0:MH, 0:1], row_a[0:MH, 0:1], 0.0, None, ALU.max)
                dve.tensor_tensor(row_m[0:MH, TP:T:TB], row_a[0:MH, TP:T:TB], m0[:, :], ALU.max)
                dve.drain()
                M = rows8[:, 0:T]
                dve.tensor_tensor_scan(M, max_restart[0:MH], row_m[0:MH], 0.0, ALU.add, ALU.max)
                dve.drain()
                M_seq = M[:, TP:T].rearrange("p (b t) -> p b t", b=NB)
                M_end = M_seq[:, :, TB - 1:TB]
                dve.tensor_tensor(row_m[0:MH], row_b[0:MH], M, ALU.add)
                dve.tensor_scalar(row_w[0:MH, 0:TP], row_a[0:MH, 0:TP], M[:, TP - 1:TP], None, ALU.subtract)
                dve.tensor_tensor(row_w[0:MH, TP:T].rearrange("p (b t) -> p b t", b=NB),
                                  row_a[0:MH, TP:T].rearrange("p (b t) -> p b t", b=NB),
                                  M_end.to_broadcast((MH, NB, TB)), ALU.subtract)
                dve.tensor_tensor(rows8[:, R_DECAY:R_INTER], m0[:, :], M[:, TP + TB - 1:T:TB], ALU.subtract)
                dve.tensor_tensor(rows8[:, R_INTER:R_EM].rearrange("p (b t) -> p b t", b=NB),
                                  m0[:, :].rearrange("p (b a) -> p b a", a=1).to_broadcast((MH, NB, TB)), M_seq,
                                  ALU.subtract).then_inc(gates_summed, 1)

            def lower_bounds():
                dve.wait_ge(lb_exp, 1)
                dve.tensor_tensor(bounds[:, 1, :], bound_cols[:, 0, :], bound_cols[:, 1, :], ALU.add)
                dve.drain()
                dve.reciprocal(bounds[:, 1, :], bounds[:, 1, :])
                dve.drain()
                for l in range(2):
                    dve.tensor_tensor(bound_cols[:, 2 + l, :], bound_cols[:, l, :], bounds[:, 1, :], ALU.mult)
                dve.drain()
                dve.tensor_tensor(bounds[:, 0, :], bound_cols[:, 2, :], bound_cols[:, 3, :], ALU.add)
                dve.drain()
                dve.tensor_tensor(bounds[:, 0, :], bounds[:, 0, :], bound_cols[:, 2, :], ALU.subtract)
                dve.drain()
                dve.tensor_scalar(bounds[:, 1, :], bounds[:, 0, :], -1.0, 1.0, ALU.mult, ALU.add)

            def keep_gate_columns():
                dve.wait_ge(rows_turned, 1)
                turned = MX[1][:, 0:2 * 3 * MH].rearrange("p (w b h) -> p w b h", w=2, b=3)
                dve.tensor_copy(gate_cols[:, :, 0:2, :], turned[:, :, 0:2, :])
                dve.tensor_copy(gate_cols[0:TS, :, 2, :], turned[0:TS, :, 2, :]).then_inc(rows_kept, 1)
                dve.drain()

            def evac_scaled(ph, n, out, scale=None, b=None):
                src = bank[(n if b is None else b)][:, 0:T]
                if scale is None:
                    return dve.tensor_tensor(out, src, rstd[:, :], ALU.mult)
                return dve.scalar_tensor_tensor(out, src, scale, rstd[:, :], ALU.mult, ALU.mult)

            def m_evac(h, s):
                out, scale = ((kT, QK_SCALE), (vT[:, 0, :], None), (vT[:, 1, :], None), (qT, None),
                              (oT[:, 0, :], None), (oT[:, 1, :], None))[s]
                dve.wait_ge(gemm_done, M_IN.base + 6 * h + s + 1)
                evac_scaled(M_IN, None, out, scale, b=s % 2).then_inc(evac_done, 1)

            def head_col(v, h):
                return v[:, bass.ds(h, 1)]

            def m1(h):
                need(dve, m_turned, h)
                dve.wait_ge(gates_exp, 1)
                dve.tensor_scalar(row_of_head, rows8, ident[0:MH, bass.ds(h, 1)], None, ALU.mult).then_inc(m_row, 1)

            def m2(h):
                dve.wait_ge(m_turned, h + 1)
                for out, src, blk, n, p in ((slice(0, TP), slice(0, TP), 0, TP, P), (slice(TP, TP + P), slice(P, TP), 1, P, P),
                                            (slice(TP + P, TP + P + TS), slice(TP, T), 2, TS, TS)):
                    last = dve.scalar_tensor_tensor(att[0:p, out], MX[0][0:p, src], gate_cols[0:p, 0, blk, bass.ds(h, 1)],
                                                    penal[0:p, out], ALU.subtract, ALU.max)
                last.then_inc(m_expo, 1)
                dve.wait_ge(m_kept, h + 1)
                for blk, p in ((0, P), (1, P), (2, TS)):
                    dve.tensor_scalar(wk[0:p, blk, :], k_tok[0:p, blk, :], gate_cols[0:p, 1, blk, bass.ds(h, 1)], None, ALU.mult)
                dve.drain()
                dve.tensor_tensor(wk_seq[0:TS], wk[0:TS, 2:3, :].to_broadcast((TS, NB, P)),
                                  seq_mask[:, :].rearrange("p (b a) -> p b a", a=1).to_broadcast((TS, NB, P)),
                                  ALU.mult).then_inc(m_wk, 1)

            def m4(h):
                dve.drain()
                dve.tensor_tensor(qw, qT[:, TP:T], spread[:, NB:], ALU.mult)
                dve.drain()
                dve.tensor_tensor(qn.rearrange("p (b t) -> p b t", b=NB), qw.rearrange("p (b t) -> p b t", b=NB),
                                  n_cols[:, :, bass.ds(h, 1)].to_broadcast((P, NB, TB)), ALU.mult).then_inc(m_qw, 1)

            def m5(h):
                dve.wait_ge(m_scores, h + 1)
                dve.wait_ge(m_weights, h + 1)
                dve.tensor_tensor(att[:, 0:TP + P], att[:, 0:TP + P], MX[0][:, 0:TP + P], ALU.mult)
                dve.tensor_tensor(att[0:TS, TP + P:], att[0:TS, TP + P:], MX[0][0:TS, TP + P:TP + P + TS],
                                  ALU.mult).then_inc(m_att, 1)

            def new_C(mx, b0):
                for i in range(2):
                    b = b0 + i
                    last = dve.scalar_tensor_tensor(C[:, b, :], C[:, b, :], spread[:, b:b + 1],
                                                    MX[mx][:, i * MDV:(i + 1) * MDV], ALU.mult, ALU.add)
                return last

            def m6(h):
                dve.wait_ge(m_abs, h + 1)
                dve.tensor_tensor(den, den, em, ALU.max)
                dve.drain()
                dve.reciprocal(den, den)
                dve.drain()
                for i in range(2):
                    last = dve.tensor_tensor(hs[:, i, :], MX[2 + i][:, 0:T], den, ALU.mult)
                last.then_inc(m_hs, 1)
                dve.wait_ge(m_new0, h + 1)
                need(dve, C_stored, 32 * h)
                dve.tensor_copy(C_p, MX[4][:, 0:MDV])
                dve.tensor_copy(n_new[:, bass.ds(h + NB * MH, 1)], MX[4][:, MDV:MDV + 1])
                dve.tensor_tensor(n_kept.rearrange("p (b a) -> p b a", a=1), n_cols[:, :, bass.ds(h, 1)],
                                  spread[:, 0:NB].rearrange("p (b a) -> p b a", a=1), ALU.mult)
                dve.drain()
                dve.tensor_tensor(n_new[:, 0:NB * MH].rearrange("p (b h) -> p b h", b=NB)[:, :, bass.ds(h, 1)],
                                  n_kept.rearrange("p (b a) -> p b a", a=1),
                                  MX[4][:, MDV + 8:MDV + 8 + NB].rearrange("p (b a) -> p b a", a=1), ALU.add)
                new_C(5, 0).then_inc(m_C0, 1)

            def m7(h):
                dve.wait_ge(m_rstd, h + 1)
                dve.wait_ge(m_sig, h + 1)
                for i in range(2):
                    dve.scalar_tensor_tensor(hs[:, i, :], hs[:, i, :], gains[:, bass.ds(GAIN_M + i + h * 2, 1)], m_rs,
                                             ALU.mult, ALU.mult)
                dve.drain()
                for i in range(2):
                    dve.tensor_tensor(g_hi[:, bass.ds(h * 2 + i, 1), :], hs[:, i:i + 1, :], oT[:, i:i + 1, :], ALU.mult)
                for i in range(2):
                    dve.tensor_tensor(oT[:, i, :], hs[:, i, :], oT[:, i, :], ALU.mult)
                dve.drain()
                for i in range(2):
                    last = dve.tensor_tensor(g_lo[:, bass.ds(h * 2 + i, 1), :], oT[:, i:i + 1, :],
                                             g_hi[:, bass.ds(h * 2 + i, 1), :].bitcast(F32), ALU.subtract)
                last.then_inc(m_gated, 1)
                dve.wait_ge(m_new1, h + 1)
                new_C(4, 2)
                new_C(5, 4).then_inc(m_C1, 1)

            def m8(h):
                dve.wait_ge(m_new2, h + 1)
                new_C(4, 6).then_inc(m_C2, 1)

            def m_body(it, before):
                for s in range(6):
                    if not (s in (1, 2) and isinstance(it, int)):
                        split_low(dve, M_IN, it, s)
                    if s == 0 and isinstance(it, int):
                        split_low(dve, M_IN, it, 1)
                        gate_rows()
                        split_low(dve, M_IN, 0, 2)
                        lower_bounds()
                        keep_gate_columns()
                    if s == 0 and before is not None:
                        m_evac(before, 5)
                        m6(before)
                    if s == 1 and before is not None:
                        m7(before)
                    if s == 2 and before is not None:
                        m8(before)
                    if s == 1 and isinstance(it, int):
                        dve.wait_ge(m_stored, 32)
                    if s:
                        m_evac(it, s - 1)
                    if s in (1, 2, 4, 5):
                        {1: m1, 2: m2, 4: m4, 5: m5}[s](it)

            m_body(0, None)
            with dve.Fori(1, MH) as it:
                m_body(it, it - 1)

            def x_evac(ph, r, it, s):
                j = it * 4 + s
                dve.wait_ge(gemm_done, ph.base + j + 1)
                add = dve.tensor_tensor(x[:, bass.ds(j, 1), :], x[:, bass.ds(j, 1), :],
                                        bank[s % ph.banks][:, 0:T].rearrange("p (a t) -> p a t", a=1), ALU.add)
                add.then_inc(evac_done, 1)
                if r is not None:
                    dve.wait_ge(evac_done, ph.base + j + 1)
                    dve.sem_inc(x_done, 1)
                    x_tile_dve(dve, r, j, s % 2, isinstance(j, int) and j == 0)

            def x_phase(ph, r, boundary):
                for s in range(4):
                    if not (ph is H_OUT and s == 1):
                        split_low(dve, ph, 0, s)
                    if s in boundary:
                        boundary[s]()
                    if s:
                        x_evac(ph, r, 0, s - 1)
                with dve.Fori(1, ph.iters) as it:
                    for s in range(4):
                        split_low(dve, ph, it, s)
                        if s:
                            x_evac(ph, r, it, s - 1)
                        else:
                            x_evac(ph, r, it - 1, 3)

            def ffn(layer, r_in, previous):
                for g, (first, n) in enumerate(GROUPS):
                    up, down = by_name[f"up{layer}{g}"], by_name[f"down{layer}{g}"]
                    pairs = layer * (FF // P) + first

                    def evac(it, s):
                        u, pair = s // 2, it * 2 + s // 2
                        dve.wait_ge(gemm_done, up.base + it * 4 + s + 1)
                        if s % 2 == 0:
                            evac_scaled(up, None, fa[:, u, :], b=s).then_inc(evac_done, 1)
                            dve.wait_ge(evac_done, up.base + it * 4 + s + 1)
                            dve.sem_inc(f_a, 1)
                            return
                        evac_scaled(up, None, fu, b=s).then_inc(evac_done, 1)
                        dve.wait_ge(f_sig_done, pairs + pair + 1)
                        dve.tensor_tensor(f_sig[:, u, :], f_sig[:, u, :], fa[:, u, :], ALU.mult)
                        dve.drain()
                        dve.tensor_tensor(g_hi[:, bass.ds(pair, 1), :], f_sig[:, u:u + 1, :],
                                          fu.rearrange("p (a t) -> p a t", a=1), ALU.mult)
                        dve.tensor_tensor(f_full[:, u, :], f_sig[:, u, :], fu, ALU.mult)
                        dve.drain()
                        dve.tensor_tensor(g_lo[:, bass.ds(pair, 1), :], f_full[:, u:u + 1, :],
                                          g_hi[:, bass.ds(pair, 1), :].bitcast(F32), ALU.subtract).then_inc(f_hidden, 1)

                    for s in range(4):
                        split_low(dve, up, 0, s)
                        if s == 0:
                            x_evac(previous, r_in if g == 0 else None, 3, 3)
                        else:
                            if g == 0 and s == 1:
                                dve.wait_ge(rstd_ready, r_in + 1)
                            evac(0, s - 1)
                    with dve.Fori(1, up.iters) as it:
                        for s in range(4):
                            split_low(dve, up, it, s)
                            evac(it if s else it - 1, s - 1 if s else 3)
                    x_phase(down, r_in + 1 if g == len(GROUPS) - 1 else None, {0: lambda: evac(up.iters - 1, 3)})
                    previous = down

            def m_end0():
                m_evac(MH - 1, 5)
                m6(MH - 1)

            def m_end1():
                m7(MH - 1)
                m8(MH - 1)

            x_phase(M_OUT, 1, {0: m_end0, 1: m_end1})
            dve.wait_ge(n_turned, 1)
            dve.tensor_copy(n_stage, MX[0][0:(NB + 1) * MH, 0:P]).then_inc(n_done, 1)
            ffn(0, 1, M_OUT)

            def h_evac(h, s):
                out, scale = ((hf, None), (hg, None), (hq, QK_SCALE), (hi_T, None))[s]
                dve.wait_ge(gemm_done, H_IN.base + 4 * h + s + 1)
                evac_scaled(H_IN, None, out, scale, b=s % 2).then_inc(evac_done, 1)

            def segment_ends(v, w):
                v = v.rearrange("p (n w) -> p n w", w=w)
                return v, v[:, :, w - 1:w].to_broadcast(tuple(v.shape))

            def pair_diffs(h, i):
                for u in range(2):
                    l = LEVELS[2 * i + u]
                    w = level_width(l)
                    A = hA[:, 0:w].rearrange("p (n r) -> p n r", r=2 * l)
                    last = dve.tensor_tensor(pair[:, u, 0:w].rearrange("p (n r) -> p n r", r=2 * l), A,
                                             A[:, :, l - 1:l].to_broadcast(tuple(A.shape)), ALU.subtract)
                last.then_inc(g_diff[i], 1)

            def pair_factors(h, i):
                dve.wait_ge(g_pairexp[i], h + 1)
                for u in range(2):
                    l = LEVELS[2 * i + u]
                    w = level_width(l)
                    first, second = halves(pair[:, u, 0:w], l)
                    dve.tensor_tensor(first, first, halves(hk[:, 0:w], l)[0], ALU.mult)
                    last = dve.tensor_tensor(second, second, halves(hq[:, 0:w], l)[1], ALU.mult)
                last.then_inc(g_pair[i], 1)

            def take_level(li, mx):
                l = LEVELS[li] if li < len(LEVELS) else 1
                w = level_width(l)
                dve.drain()
                dve.copy_predicated(scores[:, 0:TP], level_mask[:, li, 0:TP], MX[mx][:, 0:TP])
                if w > TP:
                    dve.copy_predicated(scores[0:TS, TP:T], level_mask[0:TS, li, TP:T], MX[mx][0:TS, TP:T])

            def h3(h):
                dve.wait_ge(g_fsig, h + 1)
                dve.tensor_scalar(hf, hf, bounds[:, 1, bass.ds(h, 1)], bounds[:, 0, bass.ds(h, 1)], ALU.mult, ALU.add)
                if not (isinstance(h, int) and h == 0):
                    dve.tensor_copy(gate_before, gate)
                dve.drain()
                dve.tensor_scalar(hk, hf, -1.0, 1.0, ALU.mult, ALU.add).then_inc(g_f, 1)
                dve.scalar_tensor_tensor(gate, hg, gains[:, bass.ds(GAIN_H + h, 1)], hg_sig, ALU.mult, ALU.mult)

            def h4(h):
                dve.wait_ge(g_logf, h + 1)
                dve.tensor_tensor_scan(hA, restart[:, :], h_logf, 0.0, ALU.mult, ALU.add)
                dve.drain()
                for cols, w in ((slice(0, TP), SEG), (slice(TP, T), TB)):
                    A, end = segment_ends(hA[:, cols], w)
                    last = dve.tensor_tensor(k_exp[:, cols].rearrange("p (n w) -> p n w", w=w), end, A, ALU.subtract)
                last.then_inc(g_sums, 1)
                pair_diffs(h, 0)
                dve.wait_ge(g_exps, h + 1)
                dve.tensor_tensor(k0, hk, k_exp, ALU.mult)
                dve.tensor_tensor(q0, hq, q_exp, ALU.mult).then_inc(g_factors, 1)
                pair_factors(h, 0)

            def e(i):
                return q_exp[:, i * SEG + SEG - 1:(i + 1) * SEG]

            def h5(h):
                dve.wait_ge(g_p[0], h + 1)
                pair_diffs(h, 1)
                dve.tensor_copy(scores[0:SEG, 0:TP].rearrange("p (a b c) -> p a b c", a=2, b=2)[:, :, 1, :],
                                MX[1][0:SEG, 0:2 * SEG].rearrange("p (a c) -> p a c", a=2))
                dve.tensor_scalar(k0[:, 0:SEG], k0[:, 0:SEG], e(1), None, ALU.mult)
                dve.tensor_scalar(k0[:, 2 * SEG:3 * SEG], k0[:, 2 * SEG:3 * SEG], e(3), None, ALU.mult)
                dve.tensor_scalar(q_far, q0[:, 3 * SEG:TP], e(2), None, ALU.mult)
                dve.drain()
                dve.tensor_scalar(k_last, k0[:, 0:P], e(2), e(3), ALU.mult, ALU.mult)
                take_level(0, 2)
                take_level(1, 3)
                pair_factors(h, 1)

            def h6(h):
                dve.wait_ge(g_p[1], h + 1)
                pair_diffs(h, 2)
                dve.tensor_copy(scores_far, MX[1][:, 0:P])
                take_level(2, 2)
                take_level(3, 3)
                pair_factors(h, 2)

            def h7(h):
                dve.wait_ge(g_p[2], h + 1)
                apart(dve)
                take_level(4, 2)
                take_level(5, 3)
                take_level(6, 1)
                dve.wait_ge(g_kkept, h + 1)
                dve.tensor_tensor(hk_seq[0:TS], hk_tok[0:TS, 2:3, :].to_broadcast((TS, NB, P)),
                                  seq_mask[:, :].rearrange("p (b a) -> p b a", a=1).to_broadcast((TS, NB, P)),
                                  ALU.mult).then_inc(g_kseq, 1)

            def h8(h):
                dve.wait_ge(g_o, h + 1)
                need(dve, S_stored, 32 * h)
                dve.tensor_copy(S_p, MX[4][:, 0:P])
                dve.tensor_tensor(S, S, q_exp[:, TP + TB - 1:T:TB].rearrange("p (b a) -> p b a", a=1).to_broadcast((P, NB, P)),
                                  ALU.mult)
                dve.drain()
                for i, mx in enumerate((0, 2)):
                    last = dve.tensor_tensor(S[:, 4 * i:4 * i + 4, :], S[:, 4 * i:4 * i + 4, :],
                                             MX[mx][:, :].rearrange("p (b v) -> p b v", b=4), ALU.add)
                last.then_inc(g_S, 1)

            def h9(h, gate_of):
                dve.wait_ge(g_rstd, h + 1)
                dve.tensor_tensor(h_y, MX[5][:, 0:T], h_rs, ALU.mult)
                dve.drain()
                dve.tensor_tensor(h_y, h_y, gate_of, ALU.mult).then_inc(g_full, 1)
                dve.wait_ge(g_hi_done, h + 1)
                dve.tensor_tensor(g_lo[:, bass.ds(h, 1), :], h_y.rearrange("p (a t) -> p a t", a=1),
                                  g_hi[:, bass.ds(h, 1), :].bitcast(F32), ALU.subtract).then_inc(g_gated, 1)

            def h_tail(slot, one_back, two_back, gate_of=gate_before):
                if slot == 0:
                    if two_back is not None:
                        h8(two_back)
                    if one_back is not None:
                        h4(one_back)
                if slot == 1:
                    if two_back is not None:
                        h9(two_back, gate_of)
                    if one_back is not None:
                        h5(one_back)
                if slot == 2 and one_back is not None:
                    h6(one_back)
                if slot == 3 and one_back is not None:
                    h7(one_back)

            def h_body(it, one_back, two_back):
                for s in range(4):
                    split_low(dve, H_IN, it, s)
                    if s:
                        h_evac_late = s - 1
                        if not (s == 3 and one_back is not None):
                            if s == 1 and one_back is None:
                                dve.wait_ge(rstd_ready, 3)
                            h_evac(it, h_evac_late)
                    elif one_back is not None:
                        h_evac(one_back, 3)
                    else:
                        x_evac(by_name["down02"], 2, 3, 3)
                    h_tail(s, one_back, two_back)
                    if s == 3:
                        if one_back is not None:
                            h_evac(it, 2)
                        h3(it)

            dve.wait_ge(n_stored, 32)
            dve.memset(scores, 0.0)
            h_body(0, None, None)
            h_body(1, 0, None)
            with dve.Fori(2, HH) as it:
                h_body(it, it - 1, it - 2)

            def h_end():
                h_evac(HH - 1, 3)
                split_low(dve, H_OUT, 0, 1)
                for slot in range(4):
                    h_tail(slot, HH - 1, HH - 2)
                for slot in range(4):
                    h_tail(slot, None, HH - 1, gate)

            x_phase(H_OUT, 3, {0: h_end})
            ffn(1, 3, H_OUT)
            x_evac(by_name["down12"], 4, 3, 3)

            dve.wait_ge(rstd_ready, 5)
            for part in range(2):
                c = slice(part * D // 2, (part + 1) * D // 2)
                for b, n in ((0, P), (2, TS)):
                    dve.tensor_scalar(y_tok[0:n, b, c], y_tok[0:n, b, c], rstd_cols[0:n, b:b + 1], None,
                                      ALU.mult).then_inc(y_scaled_dve, 1)

        @block.tensor
        def _(pe):
            pe.wait_ge(ones_ready, 1)
            behind = 3
            for j in range(KT + behind):
                if j < KT:
                    for q, (j0, j1) in enumerate(X_PARTS):
                        if j == j0:
                            pe.wait_ge(x_landed[q], 48)
                    need(pe, x_done, j - 1)
                    for b, n in enumerate((P, P, TS)):
                        last = pe.transpose(bank[j % 2][:, b * P:b * P + n], x_tok[0:n, b, j * P:(j + 1) * P], ident[0:n, 0:n])
                    last.then_inc(x_turned, 1)
                if j == 0:
                    pe.wait_ge(gains_landed, 80)
                    pe.transpose(bank[2][:, 0:7 * KT], vec_rows, ident[0:7 * KT, 0:7 * KT]).then_inc(cols_turned, 1)
                k = j - behind
                if k < 0:
                    continue
                if k == 0:
                    pe.wait_ge(wg_lo_ready, 1)
                    pe.wait_ge(cols_kept, 1)
                pe.wait_ge(x_lo_done, k + 1)
                hi, lo = w_hi[:, 1, k * P:(k + 1) * P], w_lo[:, 1, k * P:(k + 1) * P]
                pe.matmul(MX[0][:, 0:T], hi, h_hi[:, k, :], start=(k == 0), stop=False)
                pe.matmul(MX[0][:, 0:T], hi, h_lo[:, k, :], start=False, stop=False)
                last = pe.matmul(MX[0][:, 0:T], lo, h_hi[:, k, :], start=False, stop=(k == KT - 1))
            last.then_inc(gates_done, 1)
            norm_pe(pe, 0)
            pe.wait_ge(vectors_landed, 80)
            pe.transpose(bank[3][:, 0:2 * KT], bound_rows, ident[0:2 * KT, 0:2 * KT])
            pe.transpose(bank[3][:, 2 * KT:2 * KT + TS], n_rows, ident[0:TS, 0:TS]).then_inc(cols_turned, 1)

            def rows_to_columns():
                pe.wait_ge(gates_exp, 1)
                for which, row in ((0, row_a), (1, row_w)):
                    for b, n in enumerate((P, P, TS)):
                        last = pe.transpose(MX[1][0:n, which * 3 * MH + b * MH:which * 3 * MH + (b + 1) * MH],
                                            row[0:MH, b * P:b * P + n], ident[0:MH, 0:MH])
                last.then_inc(rows_turned, 1)

            def turn(mx, src, inc=None):
                for b, n in enumerate((P, P, TS)):
                    last = pe.transpose(MX[mx][0:n, b * P:(b + 1) * P], src[:, b * P:b * P + n], ident[:, :])
                return last

            def m1(h):
                pe.wait_ge(m_row, h + 1)
                need(pe, m_rstd, h)
                pe.matmul(MX[0][:, 0:R_EM], ones[0:MH, :], row_of_head[:, 0:R_EM], start=True, stop=True)
                pe.matmul(MX[1][:, 0:T], ones[0:MH, :], row_of_head[:, R_EM:], start=True, stop=True)
                pe.wait_ge(evac_done, M_IN.base + 6 * h + 1)
                turn(2, kT).then_inc(m_turned, 1)

            def m3(h):
                pe.wait_ge(m_kept, h + 1)
                pe.wait_ge(evac_done, M_IN.base + 6 * h + 3)
                turn(2, vT[:, 0, :])
                turn(3, vT[:, 1, :]).then_inc(m_vturned, 1)

            def m4(h):
                pe.wait_ge(m_expo, h + 1)
                pe.wait_ge(evac_done, M_IN.base + 6 * h + 4)
                pe.matmul(MX[0][:, 0:TP], kT[:, 0:P], qT[:, 0:TP], start=True, stop=True)
                pe.matmul(MX[0][:, TP:TP + P], kT[:, P:TP], qT[:, P:TP], start=True, stop=True)
                pe.matmul(MX[0][0:TS, TP + P:TP + P + TS], kT[:, TP:T], qT[:, TP:T], start=True, stop=True).then_inc(m_scores, 1)

            def causal(out, left, start):
                pe.matmul(out[:, 0:TP], left(0, P), att[:, 0:TP], start=start, stop=True, skip_group_check=True)
                pe.matmul(out[:, P:TP], left(1, P), att[:, TP:TP + P], start=False, stop=True, skip_group_check=True)
                return pe.matmul(out[:, TP:T], left(2, TS), att[0:TS, TP + P:], start=False, stop=True, skip_group_check=True)

            def new_C(mx, b0):
                for i in range(2):
                    last = pe.matmul(MX[mx][:, i * MDV:(i + 1) * MDV], wk_seq[0:TS, b0 + i, :], v_tok[0:TS, 2, :],
                                     start=True, stop=True)
                return last

            def old_states(h, k):
                if k == 6:
                    pe.wait_ge(m_qw, h + 1)
                    pe.wait_ge(m_vkept, h + 1)
                    pe.wait_ge(C_landed, 16 * (h + 1))
                b = k - 6
                if 0 <= b < NB:
                    for i in range(2):
                        pe.matmul(MX[2 + i][:, TP + b * TB:TP + (b + 1) * TB], C[:, b, i * P:(i + 1) * P],
                                  qw[:, b * TB:(b + 1) * TB], start=(b == 0), stop=True, skip_group_check=True)

            def m5(h):
                pe.wait_ge(m_att, h + 1)
                causal(MX[1], lambda blk, p: ones[0:p, :], True)
                pe.matmul(MX[1][:, TP:T], ones[:, :], qn, start=False, stop=True, skip_group_check=True)
                for i in range(2):
                    last = causal(MX[2 + i], lambda blk, p: v_tok[0:p, blk, i * P:(i + 1) * P], False)
                last.then_inc(m_num, 1)
                need(pe, m_C2, h)
                pe.wait_ge(m_wk, h + 1)
                for b in range(2):
                    pe.matmul(MX[4][:, 0:MDV], wk[:, b, :], v_tok[:, b, :], start=(b == 0), stop=(b == 1))
                for b in range(2):
                    pe.matmul(MX[4][:, MDV:MDV + 1], wk[:, b, :], ones[:, 0:1], start=(b == 0), stop=(b == 1))
                pe.matmul(MX[4][:, MDV + 8:MDV + 8 + NB], wk[0:TS, 2, :], seq_mask[:, :], start=True, stop=True)
                new_C(5, 0).then_inc(m_new0, 1)

            def m6(h):
                pe.wait_ge(m_sq, h + 1)
                for i in range(2):
                    last = pe.matmul(MX[1][:, 0:T], ones[:, :], vT[:, i, :], start=(i == 0), stop=(i == 1))
                last.then_inc(m_sum, 1)
                pe.wait_ge(m_C0, h + 1)
                new_C(4, 2)
                new_C(5, 4).then_inc(m_new1, 1)

            def m7(h):
                pe.wait_ge(m_C1, h + 1)
                new_C(4, 6).then_inc(m_new2, 1)

            def m_body(it, before):
                for s in range(6):
                    if s == 2 and isinstance(it, int):
                        pe.wait_ge(evac_done, 1)
                    products(pe, M_IN, it, s, h_hi, h_lo, (lambda k: old_states(it, k)) if s == 5 else None)
                    if s == 1 and isinstance(it, int):
                        rows_to_columns()
                    if s == 0 and before is not None:
                        m6(before)
                    if s == 1 and before is not None:
                        m7(before)
                    if s in (1, 3, 4, 5):
                        {1: m1, 3: m3, 4: m4, 5: m5}[s](it)

            m_body(0, None)
            with pe.Fori(1, MH) as it:
                m_body(it, it - 1)

            def turn_y(j, parity):
                pe.wait_ge(y_gained, j + 1)
                need(pe, y_kept, j - 1)
                for b, n in enumerate((P, P, TS)):
                    last = pe.transpose(MX[parity][0:n, b * P:(b + 1) * P], y_T[:, parity, b * P:b * P + n], ident[:, :])
                last.then_inc(y_turned, 1)

            def x_phase(ph, before_k, first_tile=0):
                def between(it, s):
                    if ph is phases[-1]:
                        return lambda k: turn_y(it * 4 + s - 1, (s - 1) % 2) if k == 8 else None

                for s in range(first_tile, 4):
                    products(pe, ph, 0, s, g_hi, g_lo, before_k if s == 0 else between(0, s))
                    if ph is M_OUT and s == 0:
                        m7(MH - 1)
                with pe.Fori(1, ph.iters) as it:
                    for s in range(4):
                        products(pe, ph, it, s, g_hi, g_lo, between(it, s))

            def ffn(layer, r_in):
                for g, (first, n) in enumerate(GROUPS):
                    up, down = by_name[f"up{layer}{g}"], by_name[f"down{layer}{g}"]

                    def x_ready(k):
                        pe.wait_ge(x_lo_done, r_in * KT + k + 1)

                    for s in range(4):
                        products(pe, up, 0, s, h_hi, h_lo, x_ready if g == 0 and s == 0 else None)
                        if g == 0 and s == 0:
                            norm_pe(pe, r_in)
                    with pe.Fori(1, up.iters) as it:
                        for s in range(4):
                            products(pe, up, it, s, h_hi, h_lo)
                    hidden = layer * (FF // P) + first
                    x_phase(down, lambda k: pe.wait_ge(f_hidden, hidden + k + 1))

            def mixer_rest(k):
                if k == KT - 2:
                    m6(MH - 1)
                    pe.wait_ge(m_gated, MH)

            x_phase(M_OUT, mixer_rest)
            pe.transpose(MX[0][0:(NB + 1) * MH, 0:P], n_new[:, :], ident[:, :]).then_inc(n_turned, 1)
            ffn(0, 1)

            def level_products(mx, left, right, w):
                for c0, c1 in ((0, P), (P, TP), (TP, T)):
                    if c0 < w:
                        last = pe.matmul(MX[mx][0:c1 - c0, c0:c1], left[:, c0:c1], right[:, c0:c1], start=True, stop=True)
                return last

            def level_pair(h, i):
                pe.wait_ge(g_pair[i], h + 1)
                for u in range(2):
                    w = level_width(LEVELS[2 * i + u])
                    last = level_products(2 + u, pair[:, u, :], pair[:, u, :], w)
                return last

            def h4(h):
                pe.wait_ge(evac_done, H_IN.base + 4 * h + 4)
                turn(0, hi_T)
                pe.wait_ge(g_factors, h + 1)
                for a in range(2):
                    pe.matmul(MX[1][0:SEG, a * SEG:(a + 1) * SEG], k0[:, a * P:a * P + SEG],
                              q0[:, a * P + SEG:(a + 1) * P], start=True, stop=True)
                level_pair(h, 0).then_inc(g_p[0], 1)

            def h5(h):
                pe.wait_ge(g_pair[1], h + 1)
                for b, src in enumerate((k_last, k0[:, P:TP])):
                    pe.transpose(MX[4][:, b * P:(b + 1) * P], src, ident[:, :])
                pe.transpose(MX[4][0:TS, 2 * P:3 * P], k0[:, TP:T], ident[:, :])
                pe.matmul(MX[1][:, 0:SEG], k0[:, 0:P], q0[:, P:P + SEG], start=True, stop=True)
                pe.matmul(MX[1][:, SEG:P], k0[:, 0:P], q_far, start=True, stop=True)
                level_pair(h, 1).then_inc(g_p[1], 1)

            def h6(h):
                level_pair(h, 2)
                level_products(1, hk, hq, T).then_inc(g_p[2], 1)

            def old_S(h, k):
                if k == 4:
                    pe.wait_ge(S_landed, 16 * (h + 1))
                b = k - 4
                if 0 <= b < NB:
                    c = slice(TP + b * TB, TP + (b + 1) * TB)
                    pe.matmul(MX[5][:, c], S[:, b, :], q0[:, c], start=(b == 0), stop=True, skip_group_check=True)

            def h7(h):
                pe.wait_ge(g_kseq, h + 1)
                out = MX[5]
                pe.matmul(out[:, 0:P], i_tok[:, 0, :], scores[:, 0:P], start=False, stop=True, skip_group_check=True)
                pe.matmul(out[:, P:TP], i_tok[:, 1, :], scores[:, P:TP], start=False, stop=True, skip_group_check=True)
                pe.matmul(out[:, P:TP], i_tok[:, 0, :], scores_far, start=False, stop=True, skip_group_check=True)
                pe.matmul(out[:, TP:T], i_tok[0:TS, 2, :], scores[0:TS, TP:T], start=False, stop=True, skip_group_check=True)
                for b in range(2):
                    pe.matmul(MX[4][:, 0:P], hk_tok[:, b, :], i_tok[:, b, :], start=(b == 0), stop=(b == 1))
                for b in range(NB):
                    last = pe.matmul(MX[(0, 2)[b // 4]][:, b % 4 * P:(b % 4 + 1) * P], hk_seq[0:TS, b, :], i_tok[0:TS, 2, :],
                                     start=True, stop=True)
                last.then_inc(g_o, 1)

            def h8(h):
                pe.wait_ge(g_sq, h + 1)
                pe.wait_ge(g_S, h + 1)
                pe.matmul(MX[4][:, 0:T], ones[:, :], h_sq, start=True, stop=True).then_inc(g_sum, 1)

            def h_tail(slot, one_back, two_back):
                if slot == 0:
                    if two_back is not None:
                        h8(two_back)
                    if one_back is not None:
                        h4(one_back)
                if slot == 1 and one_back is not None:
                    if two_back is not None:
                        pe.wait_ge(g_rstd, two_back + 1)
                    h5(one_back)
                if slot == 2 and one_back is not None:
                    h6(one_back)
                if slot == 3 and one_back is not None:
                    h7(one_back)

            def h_body(it, one_back, two_back):
                for s in range(4):
                    def between(k):
                        if s == 0 and one_back is None:
                            pe.wait_ge(x_lo_done, 2 * KT + k + 1)
                        if s == 3 and one_back is not None:
                            if k == 4 and two_back is not None:
                                pe.wait_ge(g_full, two_back + 1)
                            old_S(one_back, k)

                    products(pe, H_IN, it, s, h_hi, h_lo, between)
                    if s == 0 and one_back is None:
                        norm_pe(pe, 2)
                    h_tail(s, one_back, two_back)

            pe.wait_ge(masks_ready, 1)
            h_body(0, None, None)
            h_body(1, 0, None)
            with pe.Fori(2, HH) as it:
                h_body(it, it - 1, it - 2)

            def last_heads(tile, k):
                at = (tile, k)
                if at == (0, 0):
                    h8(HH - 2)
                    h4(HH - 1)
                if at == (0, 8):
                    pe.wait_ge(g_rstd, HH - 1)
                    h5(HH - 1)
                if at == (1, 2):
                    h6(HH - 1)
                    pe.wait_ge(g_full, HH - 1)
                if tile == 1:
                    old_S(HH - 1, k)

            for s in range(2):
                pe.wait_ge(lo_done, H_OUT.base + s + 1)
                if s == 1:
                    pe.wait_ge(evac_done, H_OUT.base)
                product_steps(pe, H_OUT, s, range(KT - 2), g_hi, g_lo, lambda k: last_heads(s, k))
            h7(HH - 1)
            h8(HH - 1)
            pe.wait_ge(g_gated, HH)
            for s in range(2):
                product_steps(pe, H_OUT, s, range(KT - 2, KT), g_hi, g_lo).then_inc(gemm_done, 1)
            x_phase(H_OUT, None, 2)
            ffn(1, 3)
            turn_y(KT - 1, 1)
            pe.wait_ge(sumsq_ready, 5 * KT)
            for b, n in enumerate((P, P, TS)):
                last = pe.matmul(MX[4][0:n, b:b + 1], sumsq[:, b * P:b * P + n], ones[:, 0:1], start=True, stop=True)
            last.then_inc(sum_done, 1)


_INS = ["x_prompt", "x_sample", "state_mlstm_C", "state_mlstm_n", "state_mlstm_m", "state_hgrn_S", "norm_mix_g",
        "norm_ffn_g", "norm_final_g", "mlstm_w_in", "mlstm_b_gates", "mlstm_head_norm_g", "mlstm_w_out", "hgrn_w_in",
        "hgrn_lower_bounds", "hgrn_g_norm_g", "hgrn_w_out", "ffn_w_up", "ffn_w_down"]
_OUTS = [(1, TP, D), (NB, TB, D), (1, 1, MH, P, MDV), (1, 1, MH, P), (1, 1, MH), (1, 1, HH, P, P),
         (1, NB, MH, P, MDV), (1, NB, MH, P), (1, NB, MH), (1, NB, HH, P, P)]


def kernel(**inputs):
    import numpy as _np
    import concourse.bacc as _bacc
    from concourse import mybir as _mybir
    from concourse.bass_utils import run_bass_kernel_spmd as _run

    nc = _bacc.Bacc("TRN2", target_bir_lowering=False, num_devices=1)
    arrays, args = {}, []
    for name in _INS:
        a = _np.ascontiguousarray(inputs[name])
        arrays[f"in_{name}_dram"] = a
        args.append(nc.dram_tensor(f"in_{name}_dram", a.shape, _mybir.dt.from_np(a.dtype), kind="ExternalInput").ap())
    for i, shape in enumerate(_OUTS):
        args.append(nc.dram_tensor(f"out_{i}_dram", shape, F32, kind="ExternalOutput").ap())
    trunk(nc, *args)
    r = _run(nc, [arrays], core_ids=[0])
    return tuple(r.results[0][f"out_{i}_dram"] for i in range(len(_OUTS)))
```
